# Optimizing a Trainium2 kernel written in Bass

```python
import jax, jax.numpy as jnp
from jax import lax
import numpy as np

D_MODEL = 1024
BATCH = 1
SEQ = 512
DEPTH = 2

A_WIDTH = D_MODEL // 2
A_GROUPS = 4
A_GROUP_DIM = A_WIDTH // A_GROUPS
A_CHUNK = 128
HEAD_DIM = 64
B_HEADS = (D_MODEL // 2) // HEAD_DIM
B_KV_HEADS = 2
B_HPG = B_HEADS // B_KV_HEADS
B_WIDTH = B_HEADS * HEAD_DIM
KV_WIDTH = B_KV_HEADS * HEAD_DIM
N_BRANCH = 3
L_CMP = 32
STRIDE_CMP = 16
L_SEL = 64
N_SEL = 16
WINDOW = 256
QBLK = 128
SPLIT_SIZES = (A_WIDTH, A_WIDTH, B_WIDTH, KV_WIDTH, KV_WIDTH, KV_WIDTH, KV_WIDTH, KV_WIDTH, KV_WIDTH, B_HEADS * N_BRANCH)
IN_WIDTH = sum(SPLIT_SIZES)
POOL_WINDOWS = (2, 4, 8, 16)
POOL_GROUPS = 4
POOL_GROUP_DIM = D_MODEL // POOL_GROUPS
N_EXPERT_GROUPS = 4
EXPERTS_PER_GROUP = 8
D_EXPERT = 256
TOP_K_EXPERTS = 2
N_EVEN = (DEPTH + 1) // 2
N_ODD = DEPTH // 2
EPS = 1e-6
NEG_INF = -1e30
FORCE_SCORE = 1e4

kernel_name = 'hybrid_gmlp_nsa_pool_hmoe'

def rms_norm(x, gain):
    xf = x.astype(jnp.float32)
    y = xf * lax.rsqrt(jnp.mean(xf * xf, axis=-1, keepdims=True) + EPS)
    return (y * gain.astype(jnp.float32)).astype(x.dtype)

def masked_softmax(scores, mask):
    s = jnp.where(mask, scores.astype(jnp.float32), NEG_INF)
    return jax.nn.softmax(s, axis=-1) * mask

def chunked_spatial_gating(u, v, v_gain, w_s, b_s):
    bsz, seq = u.shape[:2]
    u = jax.nn.gelu(u, approximate=False)
    v = jax.nn.gelu(v, approximate=False).reshape(bsz, seq // A_CHUNK, A_CHUNK, A_GROUPS, A_GROUP_DIM)
    v = rms_norm(v, v_gain)
    causal = jnp.tril(jnp.ones((A_CHUNK, A_CHUNK), dtype=bool)).astype(w_s.dtype)
    z = jnp.einsum('gts,bcsgd->bctgd', w_s * causal[None], v) + b_s.T[None, None, :, :, None]
    return u * z.reshape(bsz, seq, A_WIDTH)

def native_sparse_attention(q, kc, vc, ks, vs, kw, vw, gate_logits, q_gain, k_gain, cmp_pe, w_cmp_k, w_cmp_v):
    bsz, seq = q.shape[:2]
    G, H, D = B_KV_HEADS, B_HPG, HEAD_DIM
    pos = jnp.arange(seq)
    q = rms_norm(q.reshape(bsz, seq, G, H, D), q_gain) * (HEAD_DIM ** -0.5)

    n_chunks = seq // STRIDE_CMP
    n_cmp = n_chunks - 1

    def compress(t, w):
        c = t.reshape(bsz, n_chunks, STRIDE_CMP, G, D)
        blocks = jnp.concatenate([c[:, :-1], c[:, 1:]], axis=2) + cmp_pe[None, None, :, None, :]
        return jnp.einsum('bnlgd,lde->bnge', blocks, w)

    k_cmp = rms_norm(compress(kc, w_cmp_k), k_gain[0])
    v_cmp = compress(vc, w_cmp_v)
    cmp_end = jnp.arange(n_cmp) * STRIDE_CMP + L_CMP - 1
    cmp_mask = cmp_end[None, :] <= pos[:, None]
    s_cmp = jnp.einsum('bsghd,bngd->bghsn', q, k_cmp)
    p_cmp = masked_softmax(s_cmp, cmp_mask)
    o_cmp = jnp.einsum('bghsn,bngd->bsghd', p_cmp.astype(v_cmp.dtype), v_cmp)

    n_sel = seq // L_SEL
    top = min(N_SEL, n_sel)
    i_c = jnp.arange(n_cmp)[:, None] * STRIDE_CMP
    j_s = jnp.arange(n_sel)[None, :] * L_SEL
    overlap = ((i_c < j_s + L_SEL) & (i_c + L_CMP > j_s)).astype(jnp.float32)
    imp = jnp.einsum('bghsn,nj->bgsj', p_cmp, overlap)
    blk = jnp.arange(n_sel)[None, :]
    forced = (blk == 0) | (blk == (pos // L_SEL)[:, None])
    valid = blk * L_SEL <= pos[:, None]
    imp = jnp.where(forced, FORCE_SCORE, jnp.where(valid, imp, -1.0))
    _, sel_idx = lax.top_k(imp, top)

    ks_blocks = rms_norm(ks.reshape(bsz, n_sel, L_SEL, G, D), k_gain[1]).transpose(0, 3, 1, 2, 4)
    vs_blocks = vs.reshape(bsz, n_sel, L_SEL, G, D).transpose(0, 3, 1, 2, 4)
    nqb = seq // QBLK
    q_blocks = q.reshape(bsz, nqb, QBLK, G, H, D).transpose(1, 0, 2, 3, 4, 5)
    idx_blocks = sel_idx.reshape(bsz, G, nqb, QBLK, top).transpose(2, 0, 1, 3, 4)
    b_ix = jnp.arange(bsz)[:, None, None, None]
    g_ix = jnp.arange(G)[None, :, None, None]
    offs = jnp.arange(L_SEL)

    def sel_block(args):
        qb, ib, start = args
        kg = ks_blocks[b_ix, g_ix, ib]
        vg = vs_blocks[b_ix, g_ix, ib].reshape(bsz, G, QBLK, top * L_SEL, D)
        kpos = ib[..., None] * L_SEL + offs
        qpos = start + jnp.arange(QBLK)
        mask = (kpos <= qpos[None, None, :, None, None]).reshape(bsz, G, QBLK, top * L_SEL)
        s = jnp.einsum('bqghd,bgqkld->bghqkl', qb, kg).reshape(bsz, G, H, QBLK, top * L_SEL)
        p = masked_softmax(s, mask[:, :, None])
        return jnp.einsum('bghqm,bgqmd->bqghd', p.astype(vg.dtype), vg)

    o_sel = lax.map(sel_block, (q_blocks, idx_blocks, jnp.arange(nqb) * QBLK))
    o_sel = o_sel.transpose(1, 0, 2, 3, 4, 5).reshape(bsz, seq, G, H, D)

    n_band = WINDOW // QBLK + 1
    kwb = rms_norm(kw.reshape(bsz, nqb, QBLK, G, D), k_gain[2])
    vwb = vw.reshape(bsz, nqb, QBLK, G, D)

    def band(t):
        tp = jnp.pad(t, ((0, 0), (n_band - 1, 0), (0, 0), (0, 0), (0, 0)))
        return jnp.concatenate([tp[:, i:i + nqb] for i in range(n_band)], axis=2)

    kband, vband = band(kwb), band(vwb)
    qpos = jnp.arange(nqb)[:, None] * QBLK + jnp.arange(QBLK)[None, :]
    kpos = jnp.arange(nqb)[:, None] * QBLK - (n_band - 1) * QBLK + jnp.arange(n_band * QBLK)[None, :]
    kp, qp = kpos[:, None, :], qpos[:, :, None]
    wmask = (kp <= qp) & (kp > qp - WINDOW) & (kp >= 0)
    qb_all = q.reshape(bsz, nqb, QBLK, G, H, D)
    s_w = jnp.einsum('bnqghd,bnmgd->bghnqm', qb_all, kband)
    p_w = masked_softmax(s_w, wmask)
    o_win = jnp.einsum('bghnqm,bnmgd->bnqghd', p_w.astype(vband.dtype), vband).reshape(bsz, seq, G, H, D)

    g = jax.nn.sigmoid(gate_logits).reshape(bsz, seq, G, H, N_BRANCH)
    o = g[..., 0:1] * o_cmp + g[..., 1:2] * o_sel + g[..., 2:3] * o_win
    return o.reshape(bsz, seq, B_WIDTH)

def multiscale_pool(xn, w_pool, b_pool, scale):
    bsz, seq, _ = xn.shape
    xg = xn.reshape(bsz, seq, POOL_GROUPS, POOL_GROUP_DIM)
    maxw = max(POOL_WINDOWS)
    c = jnp.cumsum(xg.astype(jnp.float32), axis=1)
    cp = jnp.pad(c, ((0, 0), (maxw, 0), (0, 0), (0, 0)))
    pooled = []
    for g, w in enumerate(POOL_WINDOWS):
        s = cp[:, maxw:, g] - cp[:, maxw - w:maxw - w + seq, g]
        cnt = jnp.minimum(jnp.arange(seq) + 1, w).astype(jnp.float32)[None, :, None]
        pooled.append(s / cnt)
    pooled = jnp.stack(pooled, axis=2).astype(xn.dtype) - xg
    y = jnp.einsum('bsgc,gce->bsge', pooled, w_pool) + b_pool
    return y.reshape(bsz, seq, D_MODEL) * scale

def hierarchical_moe(xn, w_rg, b_rg, w_re, b_re, w_gate, w_up, w_down):
    lg = (jnp.einsum('bsd,dg->bsg', xn, w_rg) + b_rg).astype(jnp.float32)
    pg = jax.nn.softmax(lg, axis=-1)
    g_sel = jnp.argmax(lg, axis=-1)
    pg_sel = jnp.max(pg, axis=-1, keepdims=True)
    g_hot = jax.nn.one_hot(g_sel, N_EXPERT_GROUPS, dtype=jnp.float32)
    le = (jnp.einsum('bsd,dge->bsge', xn, w_re) + b_re).astype(jnp.float32)
    le_sel = jnp.sum(le * g_hot[..., None], axis=2)
    top_v, top_i = lax.top_k(le_sel, TOP_K_EXPERTS)
    pe = jax.nn.softmax(top_v, axis=-1) * pg_sel
    w_in_group = jnp.sum(jax.nn.one_hot(top_i, EXPERTS_PER_GROUP, dtype=jnp.float32) * pe[..., None], axis=-2)
    combine = (g_hot[..., None] * w_in_group[:, :, None, :]).astype(xn.dtype)
    y = jnp.zeros_like(xn)
    for g in range(N_EXPERT_GROUPS):
        h = jax.nn.silu(jnp.einsum('bsd,edf->bsef', xn, w_gate[g])) * jnp.einsum('bsd,edf->bsef', xn, w_up[g])
        y = y + jnp.einsum('bsef,efd->bsd', h * combine[:, :, g, :, None], w_down[g])
    return y

def setup_inputs(seed: int = 0) -> dict:
    key = jax.random.key(seed)
    keys = iter(jax.random.split(key, 32))

    def nrm(shape, scale):
        return jax.random.normal(next(keys), shape, jnp.float32) * scale

    def gain(shape, noise=0.05):
        return 1.0 + noise * jax.random.normal(next(keys), shape, jnp.float32)

    E, O, L = N_EVEN, N_ODD, DEPTH
    NG, EPG, F = N_EXPERT_GROUPS, EXPERTS_PER_GROUP, D_EXPERT
    return {
        'x': nrm((BATCH, SEQ, D_MODEL), 1.0),
        'mix_norm_even': gain((E, D_MODEL)),
        'w_in': nrm((E, D_MODEL, IN_WIDTH), D_MODEL ** -0.5),
        'a_v_gain': gain((E, A_GROUPS, A_GROUP_DIM)),
        'a_w_s': nrm((E, A_GROUPS, A_CHUNK, A_CHUNK), 0.5 * A_CHUNK ** -0.5),
        'a_b_s': gain((E, A_GROUPS, A_CHUNK), 0.1),
        'q_gain': gain((E, HEAD_DIM)),
        'k_gain': gain((E, N_BRANCH, HEAD_DIM)),
        'cmp_pe': nrm((E, L_CMP, HEAD_DIM), 0.5),
        'w_cmp_k': nrm((E, L_CMP, HEAD_DIM, HEAD_DIM), (L_CMP * HEAD_DIM) ** -0.5),
        'w_cmp_v': nrm((E, L_CMP, HEAD_DIM, HEAD_DIM), (L_CMP * HEAD_DIM) ** -0.5),
        'w_out': nrm((E, D_MODEL, D_MODEL), D_MODEL ** -0.5),
        'mix_norm_odd': gain((O, D_MODEL)),
        'w_pool': nrm((O, POOL_GROUPS, POOL_GROUP_DIM, POOL_GROUP_DIM), POOL_GROUP_DIM ** -0.5),
        'b_pool': nrm((O, POOL_GROUPS, POOL_GROUP_DIM), 0.01),
        'pool_scale': gain((O, D_MODEL), 0.1),
        'ffn_norm': gain((L, D_MODEL)),
        'w_router_group': nrm((L, D_MODEL, NG), D_MODEL ** -0.5),
        'b_router_group': nrm((L, NG), 0.01),
        'w_router_expert': nrm((L, D_MODEL, NG, EPG), D_MODEL ** -0.5),
        'b_router_expert': nrm((L, NG, EPG), 0.01),
        'w_exp_gate': nrm((L, NG, EPG, D_MODEL, F), D_MODEL ** -0.5),
        'w_exp_up': nrm((L, NG, EPG, D_MODEL, F), D_MODEL ** -0.5),
        'w_exp_down': nrm((L, NG, EPG, F, D_MODEL), F ** -0.5),
    }

def reference(x, mix_norm_even, w_in, a_v_gain, a_w_s, a_b_s, q_gain, k_gain, cmp_pe, w_cmp_k, w_cmp_v, w_out,
              mix_norm_odd, w_pool, b_pool, pool_scale, ffn_norm, w_router_group, b_router_group,
              w_router_expert, b_router_expert, w_exp_gate, w_exp_up, w_exp_down):
    split_points = [int(v) for v in np.cumsum(SPLIT_SIZES)[:-1]]
    for layer in range(DEPTH):
        i = layer // 2
        if layer % 2 == 0:
            xn = rms_norm(x, mix_norm_even[i])
            proj = jnp.einsum('bsd,de->bse', xn, w_in[i])
            au, av, q, kc, vc, ks, vs, kw, vw, gl = jnp.split(proj, split_points, axis=-1)
            ya = chunked_spatial_gating(au, av, a_v_gain[i], a_w_s[i], a_b_s[i])
            yb = native_sparse_attention(q, kc, vc, ks, vs, kw, vw, gl, q_gain[i], k_gain[i], cmp_pe[i],
                                         w_cmp_k[i], w_cmp_v[i])
            x = x + jnp.einsum('bse,ed->bsd', jnp.concatenate([ya, yb], axis=-1), w_out[i])
        else:
            x = x + multiscale_pool(rms_norm(x, mix_norm_odd[i]), w_pool[i], b_pool[i], pool_scale[i])
        x = x + hierarchical_moe(rms_norm(x, ffn_norm[layer]), w_router_group[layer], b_router_group[layer],
                                 w_router_expert[layer], b_router_expert[layer], w_exp_gate[layer],
                                 w_exp_up[layer], w_exp_down[layer])
    return x


_drawn_inputs = setup_inputs


def setup_inputs(seed=0):
    import zlib

    import numpy as np

    out = dict(_drawn_inputs(seed))
    spreads = {}
    factors = {'a_v_gain': 3.126,
     'k_gain': 3.462,
     'b_pool': 4.148,
     'b_router_group': 3.554,
     'b_router_expert': 2.988}
    for name, (base, spread) in spreads.items():
        noise = np.random.default_rng([zlib.crc32(name.encode()), seed]).standard_normal(out[name].shape)
        drawn = base * np.exp(spread * noise) if base else spread * noise
        out[name] = __import__('jax').numpy.asarray(drawn.astype(out[name].dtype))
    for name, factor in factors.items():
        out[name] = (out[name] * factor).astype(out[name].dtype)
    return out
```

```python
import concourse.bass as bass
from concourse import mybir
from contextlib import ExitStack

F32 = mybir.dt.float32
BF16 = mybir.dt.bfloat16
I32 = mybir.dt.int32
ALU = mybir.AluOpType
ACT = mybir.ActivationFunctionType
AX = mybir.AxisListType.X

P = 128
D = 1024
SEQ = 512
NB = SEQ // P
KD = D // P
NEG = -1e30
EPS = 1e-6
HD = 64
NH = 8
LAYERS = 2
NE = 32
FE = 256
TILE = 64
STEP_TILES = 4
STEPS = NE // STEP_TILES
MAX_OVER = 16
MAX_STEPS = STEPS + MAX_OVER // STEP_TILES
PAIRS = 2 * MAX_STEPS
EMPTY = 4096.0


def build(nc, t):
    ctx = ExitStack()
    with ctx:
        def sb(name, cols, dt=F32, parts=P):
            return ctx.enter_context(nc.sbuf_tensor(name, [parts, cols], dt))

        def sem(name):
            return ctx.enter_context(nc.semaphore(name))

        def sems(name, n):
            return [sem(f"{name}{i}") for i in range(n)]

        X = sb("x_rows", NB * D)
        NORM = sb("norm", 2 * NB * D)
        TMP = sb("tmp", 6144)
        W0 = sb("w_pair0", 12288)
        W1 = sb("w_pair1", 12288)
        R = sb("rest", 8192)
        ident = sb("ident", P)
        identb = sb("identb", P, BF16)
        mask_causal = sb("mask_causal", P, BF16)
        mask_window = sb("mask_window", P, BF16)
        earlier = sb("earlier", P, BF16)
        ones = sb("ones", P, BF16)
        prefix = sb("prefix", 2 * NE, BF16, NE)
        col128 = sb("col128", P)
        col32 = sb("col32", 32)
        tok_id = sb("tok_id", 2 * NB)
        slot0 = sb("slot0", NE)
        over0 = sb("over0", NE)
        bounds = sb("bounds", 8)
        small = sb("small", 2 * NB * 32)
        cmp_add = small[:, 0:128]
        cmp_01 = small[:, 128:256]
        nmax = small[:, 0:64]
        psum_row = small[:, 64:128]
        coef = small[:, 128:192]
        gains = sb("gains", 4 * KD)
        r_bias = sb("r_bias", LAYERS * 36)
        w_r = sb("w_r", KD * 36)
        b_s = sb("b_s", 4)
        q_gain = sb("q_gain", 1)
        k_gain = sb("k_gain", 2)
        kc_gain = sb("kc_gain", HD)
        pe = sb("pe", 32)
        ssq = sb("ssq", 4 * NB)
        std = sb("std", 4 * NB)
        rstd = sb("rstd", 4 * NB)
        hsq = sb("hsq", 48)
        hstd = sb("hstd", 48)
        hrstd = sb("hrstd", 48)
        vsq = sb("vsq", 16)
        vstd = sb("vstd", 16)
        vrstd = sb("vrstd", 16)
        csq = sb("csq", 4)
        gate = sb("gate", NB * 24)
        cmax = sb("cmax", NB * NH)
        csum = sb("csum", NB * NH)
        weight = TMP[:, 5888:5896]
        gather_at = TMP[:, 5896:5896 + PAIRS + 2].bitcast(I32)
        scatter_at = TMP[:, 5928:5928 + PAIRS].bitcast(I32)
        gather_now = [sb(f"gather_now{s}", 1, I32) for s in range(2)]
        scatter_now = [sb(f"scatter_now{s}", 1, I32) for s in range(2)]
        over_tab = sb("over_tab", MAX_OVER + 1, I32)

        ps = [ctx.enter_context(nc.psum_tensor(f"ps{i}", [P, 2, 512], F32)) for i in range(4)]

        def bank(i):
            return ps[i // 2][:, i % 2, :]

        norm_dram = nc.dram_tensor("norm_rows", [SEQ, D], F32).ap()
        out_dram = nc.dram_tensor("expert_rows", [2 * SEQ, D], F32).ap()

        x3 = X[:, :].rearrange("p (b d) -> p b d", b=NB)
        xs = NORM[:, 0:4096].rearrange("p (b d) -> p b d", b=NB)
        xT = NORM[:, 4096:8192].rearrange("p (k t) -> p k t", k=KD)
        YL = NORM[:, :].rearrange("p (k b d) -> p k b d", k=2, b=NB)
        wcmp = NORM[:, 0:4096].rearrange("p (w l e) -> p w l e", w=2, l=32)
        win = [W1[:, i * 4096:(i + 1) * 4096] for i in range(2)]
        kv = W1[:, 8192:11264].rearrange("p (b c) -> p b c", b=NB)
        ws_raw = W1[:, 11264:11776].rearrange("p (g s) -> p g s", g=4)
        wsT = W1[:, 11776:12288].rearrange("p (g t) -> p g t", g=4)
        wout = W1[:, 0:8192].rearrange("p (k n) -> p k n", k=KD)
        u = TMP[:, 0:2048].rearrange("p (b c) -> p b c", b=NB)
        v = TMP[:, 2048:4096].rearrange("p (b c) -> p b c", b=NB)
        prob = TMP[:, 4096:6144].rearrange("p (u h n) -> p u h n", u=2, h=2)
        squares = TMP[:, 4096:6144]
        cmp_in = [TMP[:, 4096 + 1024 * i:5120 + 1024 * i].rearrange("p (l n) -> p l n", l=32) for i in range(2)]
        vbd = TMP[:, 4096:4608].rearrange("p (g c) -> p g c", g=2)
        kcn = TMP[:, 4608:4736]
        kcsq = TMP[:, 4736:4800]
        kcT = TMP[:, 4864:4896]
        q = R[:, 0:2048].rearrange("p (b c) -> p b c", b=NB)
        yb = q
        qT = NORM[:, 0:4096].rearrange("p (g i t) -> p g i t", g=2, i=4)
        kT = R[:, 4096:5120].rearrange("p (r t) -> p r t", r=2)
        rawT = R[:, 5120:6144].rearrange("p (r t) -> p r t", r=2)
        v_gain = W1[:, 11776:12288]
        pT = R[:, 6144:8192].rearrange("p (u a h t) -> p u a h t", u=2, a=4, h=2)
        squares2 = R[:, 6144:8192]
        sc = R[:, 6144:7168].rearrange("p (b h n) -> p b h n", b=NB, h=NH)
        pcT = R[:, 7168:8192].rearrange("p (j t) -> p j t", j=8)
        xg = [TMP[:, s * 1024:(s + 1) * 1024] for s in range(2)]
        xgT = TMP[:, 2048:3072].rearrange("p (k t) -> p k t", k=KD)
        sg = TMP[:, 3072:3328]
        hid = TMP[:, 3328:3584]
        hidT = TMP[:, 3584:3840].rearrange("p (j t) -> p j t", j=2)
        ys = [TMP[:, 3840 + s * 1024:4864 + s * 1024] for s in range(2)]
        WP = [W0, W1]
        gu = [w[:, 0:8192].rearrange("p (a m n) -> p a m n", a=2, m=2) for w in WP]
        dn = [w[:, 8192:12288].rearrange("p (a n) -> p a n", a=2) for w in WP]
        w_pool = R[:, 3584:5632].rearrange("p (c e) -> p c e", c=8)
        band = R[:, 5632:6144].rearrange("p (g t) -> p g t", g=4)
        band0 = R[:, 6144:6656].rearrange("p (g t) -> p g t", g=4)
        spill = R[:, 6656:6720].rearrange("p (g t) -> p g t", g=4)
        pool_b = R[:, 6720:7744]
        pool_sc = R[:, 0:1024]
        gain_v = gains[:, :].rearrange("p (n k) -> p n k", n=4)

        wg_rows = t["w_exp_gate"].rearrange("l g e (p k) f -> (l g e) p (k f)", k=KD)
        wu_rows = t["w_exp_up"].rearrange("l g e (p k) f -> (l g e) p (k f)", k=KD)
        wd_rows = t["w_exp_down"].rearrange("l g e (p j) d -> (l g e) p (j d)", j=2)

        CH = [("q", 1024, 512), ("kc_vc_ks_vs", 1536, 512), ("kw_vw_gates", 2048, 280),
              ("a_v", 512, 512), ("a_u", 0, 512)]
        UNITS = [(br, b, i) for b in range(NB) for br in range(2) for i in range(4)]

        def first_key(br, b):
            return 0 if br == 0 else max(0, b - 2)

        def key_blocks(un):
            br, b, _ = un
            return b + 1 - first_key(br, b)

        s_x = sems("x_loaded", NB)
        s_w = sems("win_loaded", len(CH))
        s_gain = sem("first_gain_loaded")
        s_small = sem("small_loaded")
        s_wr = sem("router_loaded")
        s_wcmp = sem("wcmp_loaded")
        s_ws = sem("ws_loaded")
        s_wout = sem("wout_loaded")
        s_poolw = sem("pool_weights_loaded")
        s_pool0 = sem("pool_consts")
        s_const = sem("consts")
        s_sq = sem("norm_squares")
        s_ms = sem("norm_mean")
        s_sd = sem("norm_std")
        s_rs = sem("norm_rstd")
        s_xs = sems("norm_rows", NB)
        s_tp = sem("norm_transposed")
        s_ta = sem("norm_evac_act")
        s_tv = sem("norm_evac_dve")
        s_pj = sem("proj_done")
        s_pe_ = sem("proj_evac")
        s_hs = sem("head_squares")
        s_hm = sem("head_mean")
        s_hd = sem("head_std")
        s_qk_n = sem("qk_normed")
        s_ge = sem("gate_exp")
        s_vs = sem("v_squares")
        s_vm = sem("v_mean")
        s_vd = sem("v_std")
        s_vn = sem("v_normed")
        s_vg = sem("v_gained")
        s_mt = sem("mix_transposed")
        s_mta = sem("mix_evac_act")
        s_mtv = sem("mix_evac_dve")
        s_wsm = sem("ws_masked")
        s_ci = sem("cmp_inputs")
        s_cz = sem("cmp_pads")
        s_cm = sem("cmp_done")
        s_cr = sem("cmp_read")
        s_k2 = sem("kcmp_mean")
        s_k3 = sem("kcmp_std")
        s_kn = sem("kcmp_normed")
        s_kt = sem("kcmp_transposed")
        s_kv = sem("kcmp_evac")
        s_vb = sem("vbd_ready")
        s_zd = sem("z_done")
        s_ya = sem("ya_ready")
        s_cs = sem("cmp_scores")
        s_c1 = sem("cmp_shifted")
        s_c2 = sem("cmp_exp")
        s_c3 = sem("cmp_prob")
        s_c4 = sem("cmp_prob_transposed")
        s_c5 = sem("cmp_prob_evac")
        s_c6 = sem("cmp_out")
        s_c7 = sem("cmp_out_read")
        s_qk = sem("scores_done")
        s_mx = sem("row_max_ready")
        s_ex = sem("probs_ready")
        s_pt = sem("probs_transposed")
        s_pd = sem("probsT_dve")
        s_pa = sem("probsT_act")
        s_pv = sem("values_done")
        s_o = sem("values_added")
        s_yt = sem("mixed_transposed")
        s_yv = sem("mixedT_dve")
        s_yc = sem("mixedT_act")
        s_op = sem("out_proj_done")
        s_x1 = sem("mixer_added")
        s_st = sem("norm_rows_stored")
        s_lg = sem("logits_done")
        s_r1 = sem("route_shifted")
        s_r2 = sem("route_exp")
        s_r3 = sem("route_onehot")
        s_r4 = sem("route_rank")
        s_r5 = sem("route_over")
        s_r6 = sem("route_prefix")
        s_r7 = sem("route_slots")
        s_r8 = sem("route_table_done")
        s_tab = sem("route_table_ready")
        s_gn = sems("gather_index", LAYERS)
        s_sn = sems("scatter_index", LAYERS)
        s_xg = [sems(f"gathered{l}_", 2) for l in range(LAYERS)]
        s_xp = sems("slots_transposed", LAYERS)
        s_xe = sems("slotsT_ready", LAYERS)
        s_gul = [sems(f"gate_up_loaded{l}_", 2) for l in range(LAYERS)]
        s_dnl = [sems(f"down_loaded{l}_", 2) for l in range(LAYERS)]
        s_gud = [sems(f"gate_up_done{l}_", 2) for l in range(LAYERS)]
        s_sil = sems("silu_ready", LAYERS)
        s_h = sems("hidden_ready", LAYERS)
        s_ht = sems("hidden_transposed", LAYERS)
        s_he = sems("hiddenT_ready", LAYERS)
        s_y = [sems(f"down_done{l}_", 2) for l in range(LAYERS)]
        s_yr = [sems(f"expert_rows_ready{l}_", 2) for l in range(LAYERS)]
        s_yo = [sems(f"expert_rows_stored{l}_", 2) for l in range(LAYERS)]
        s_yf = sems("expert_rows_free", LAYERS)
        s_zero = sem("gather_buffers_zeroed")
        s_all = sem("experts_done")
        s_yl = sems("expert_out_loaded", NB)
        s_cb = sem("experts_added")
        s_pt2 = sem("pooled")
        s_p2v = sem("pooled_dve")
        s_p2a = sem("pooled_act")
        s_ps = sem("pool_scaled")
        s_pb = sem("pool_bias_added")
        s_po = sem("pool_done")
        s_x3 = sem("pool_added")
        s_out = sem("out_stored")
        s_av = sem("act_self")
        s_dv = sem("dve_self")
        s_gp = sem("pool_self")
        s_pass = sem("pool_passed")

        SMALL = 16 * 14
        TN = {0: 0, 1: 1, 3: 2}

        def x_ready(n, b):
            return [(s_x[b], 16), (s_x1, 2 * (b + 1)), (s_cb, b + 1), (s_x3, b + 1)][n]

        rt, at = {}, [0]

        def take(name, n, dt=F32):
            cols = n if dt != BF16 else (n + 1) // 2
            view = R[:, at[0]:at[0] + cols]
            rt[name] = view if dt == F32 else view.bitcast(dt)
            at[0] += cols
            return rt[name]

        take("lgt", 144); take("exin", 20); take("expo", 20); take("gmax", 4); take("eq4", 16); take("t4", 16)
        take("gmin", 4); take("ghot", 16); take("prod", 128); take("les", 32); take("m1", 4); take("eq8", 32)
        take("t8", 32); take("mi", 4); take("h1", 32); take("les2", 32); take("m2", 4); take("h2", 32)
        take("O", 256); take("Ob", 128, BF16); take("sE", 4); take("p1", 4); take("sl", 8); take("sli", 8, I32)
        take("pmi", 8, I32); take("pci", 8, I32); take("pm", 8); take("pc", 8); take("cnt", 1); take("ovc", 8)
        take("ovs", 1); take("ovB", 128, BF16); take("B", 32); take("ge", 128); take("A", 128); take("pS", 256)
        take("tabc", 512); take("tabr", 16); take("nst", 8); take("nsr", 1); take("tabf", PAIRS); take("tge", PAIRS)
        take("OA", 1024); take("OC", 8 * PAIRS)
        assert at[0] <= 3584, at[0]

        def load_router(eng, l):
            wr = w_r[:, :].rearrange("p (k c) -> p k c", k=KD)
            eng.dma_start(wr[:, :, 0:4], t["w_router_group"][l].rearrange("(p k) g -> p k g", k=KD))\
               .then_inc(s_wr, 16)
            eng.dma_start(wr[:, :, 4:36], t["w_router_expert"][l].rearrange("(p k) g e -> p k (g e)", k=KD))\
               .then_inc(s_wr, 16)

        block = ctx.enter_context(nc.Block())

        @block.sync
        def _(sp):
            gn = [t["mix_norm_even"][0], t["ffn_norm"][0], t["mix_norm_odd"][0], t["ffn_norm"][1]]

            def load_gain(n):
                if n == 2:
                    return sp.dma_start(gain_v[:, n, :].rearrange("p (g i) -> p g i", g=4),
                                        gn[n].rearrange("(g p i) -> p g i", g=4, i=2))
                return sp.dma_start(gain_v[:, n, :], gn[n].rearrange("(p k) -> p k", k=KD))

            for b in range(NB):
                sp.dma_start(x3[:, b, :], t["x"][0, b * P:(b + 1) * P, :]).then_inc(s_x[b], 16)
            load_gain(0).then_inc(s_gain, 16)

            def load_win(ch):
                _, c0, n = CH[ch]
                dst = win[ch % 2][:, 0:KD * n].rearrange("p (k n) -> p k n", k=KD)
                src = t["w_in"][0].rearrange("(p k) n -> p k n", k=KD)[:, :, c0:c0 + n]
                sp.dma_start(dst, src).then_inc(s_w[ch], 16)

            def load_gate_up(l, s, tile0, which=(0, 1)):
                for a in which:
                    for m, rows in enumerate((wg_rows, wu_rows)):
                        sp.dma_start(gu[s][:, a, m, :], rows[bass.ds(tile0[a], 1)]
                                     .rearrange("a p f -> p (a f)")).then_inc(s_gul[l][s], 16)

            def load_down(l, s, tile0):
                for a in range(2):
                    sp.dma_start(dn[s][:, a, :], wd_rows[bass.ds(tile0[a], 1)]
                                 .rearrange("a p f -> p (a f)")).then_inc(s_dnl[l][s], 16)

            load_win(0)
            load_win(1)
            for n in (1, 2, 3):
                load_gain(n).then_inc(s_small, 16)
            rb = r_bias[:, :].rearrange("p (l c) -> p l c", l=LAYERS)
            sp.dma_start(rb[:, :, 0:4], t["b_router_group"].unsqueeze(0).to_broadcast([P, LAYERS, 4])).then_inc(s_small, 16)
            sp.dma_start(rb[:, :, 4:36], t["b_router_expert"].rearrange("l g e -> l (g e)").unsqueeze(0)
                          .to_broadcast([P, LAYERS, 32])).then_inc(s_small, 16)
            sp.dma_start(v_gain, t["a_v_gain"].rearrange("o g d -> o (g d)").to_broadcast([P, 512])).then_inc(s_small, 16)
            sp.dma_start(kc_gain[:, :], t["k_gain"][0, 0:1, :].to_broadcast([P, HD])).then_inc(s_small, 16)
            with nc.allow_non_contiguous_dma(reason="a few columns of small vectors"):
                for h in range(2):
                    r = slice(HD * h, HD * h + HD)
                    sp.dma_start(q_gain[r, :], t["q_gain"].rearrange("o d -> d o")).then_inc(s_small, 16)
                    sp.dma_start(k_gain[r, :], t["k_gain"][0, 1:3, :].rearrange("r d -> d r")).then_inc(s_small, 16)
                sp.dma_start(b_s[:, :], t["a_b_s"][0].rearrange("g t -> t g")).then_inc(s_small, 16)
                for h in range(2):
                    sp.dma_start(pe[HD * h:HD * h + HD, :], t["cmp_pe"][0].rearrange("l d -> d l")).then_inc(s_small, 16)
            load_router(sp, 0)
            sp.dma_start(ws_raw, t["a_w_s"][0].rearrange("g t s -> t g s")).then_inc(s_ws, 16)
            load_gate_up(0, 0, [0, 1])
            load_down(0, 0, [0, 1])
            for ch in range(2, len(CH)):
                sp.wait_ge(s_pj, 4 * (ch - 1))
                load_win(ch)
                if ch == 2:
                    sp.wait_ge(s_tp, 2 * NB)
                    for w, name in enumerate(("w_cmp_k", "w_cmp_v")):
                        for g in range(2):
                            sp.dma_start(wcmp[64 * g:64 * g + 64, w], t[name][0].rearrange("l d e -> d l e"))\
                              .then_inc(s_wcmp, 16)
            sp.wait_ge(s_pj, 20)
            sp.dma_start(wout, t["w_out"][0].rearrange("(k p) n -> p k n", p=P)).then_inc(s_wout, 16)

            for l in range(LAYERS):
                n = 1 + 2 * l
                if l == 0:
                    sp.wait_ge(s_op, 2 * NB)
                    load_gate_up(0, 1, [2, 3], (0,))
                for b in range(NB):
                    sp.wait_ge(s_xs[b], n + 1)
                    sp.dma_start(norm_dram[b * P:(b + 1) * P, :], xs[:, b, :]).then_inc(s_st, 16)
                if l == 0:
                    load_gate_up(0, 1, [2, 3], (1,))
                    load_down(0, 1, [2, 3])
                if l == 0:
                    sp.wait_ge(s_x1, 2 * NB)
                    sp.dma_start(w_pool.rearrange("p (g i) e -> p g i e", g=4),
                                 t["w_pool"][0].rearrange("g (p i) e -> p g i e", i=2)).then_inc(s_poolw, 16)
                    sp.dma_start(pool_b, t["b_pool"].rearrange("o g e -> o (g e)").to_broadcast([P, D]))\
                      .then_inc(s_poolw, 16)

                def steps(j, rows):
                    for s in range(2):
                        first, second = rows(s)
                        sp.wait_ge(s_gud[l][s], j)
                        load_gate_up(l, s, [first, second])
                        sp.wait_ge(s_y[l][s], j)
                        load_down(l, s, [first, second])

                with sp.Fori(1, STEPS) as j:
                    steps(j, lambda s: [l * NE + STEP_TILES * j + 2 * s + a for a in range(2)])
                sp.wait_ge(s_tab, l + 1)
                n_steps = sp.value_load(over_tab[0:1, MAX_OVER:MAX_OVER + 1], min_val=STEPS, max_val=MAX_STEPS)
                if l == 0:
                    sp.dma_start(pool_sc, t["pool_scale"].to_broadcast([P, D])).then_inc(s_poolw, 16)
                    load_router(sp, 1)
                with sp.Fori(STEPS, MAX_STEPS) as j:
                    with sp.If(n_steps > j):
                        def rows(s):
                            return [l * NE + sp.value_load(
                                over_tab[0:1, bass.ds(STEP_TILES * (j - STEPS) + 2 * s + a, 1)],
                                min_val=0, max_val=NE - 1) for a in range(2)]
                        steps(j, rows)
                sp.wait_ge(s_all, l + 1)
                for b in range(NB):
                    for k in range(2):
                        sp.dma_start(YL[:, k, b, :], out_dram[k * SEQ + b * P:k * SEQ + (b + 1) * P, :])\
                          .then_inc(s_yl[b], 16)
                if l == 0:
                    for s in range(2):
                        sp.wait_ge(s_gud[0][s], n_steps)
                        load_gate_up(1, s, [NE + 2 * s, NE + 2 * s + 1])
                        sp.wait_ge(s_y[0][s], n_steps)
                        load_down(1, s, [NE + 2 * s, NE + 2 * s + 1])
            for b in range(NB):
                sp.wait_ge(s_cb, NB + b + 1)
                sp.dma_start(t["out"][0, b * P:(b + 1) * P, :], x3[:, b, :]).then_inc(s_out, 16)
            sp.wait_ge(s_out, 16 * NB)

        @block.gpsimd
        def _(pool):
            g = nc.gpsimd
            count = [0]

            def link(ins):
                count[0] += 1
                ins.then_inc(s_gp, 1)
                pool.wait_ge(s_gp, count[0])

            def select(m, fill, base, pattern, cm, op=ALU.is_ge):
                link(g.affine_select(out=m, in_=m, compare_op=op, fill=fill, base=base, pattern=pattern,
                                     channel_multiplier=cm))

            g.memset(ident[:, :], 0.0)
            g.memset(mask_causal[:, :], 0.0)
            g.memset(mask_window[:, :], 0.0)
            g.memset(ones[:, :], 1.0)
            g.memset(earlier[:, :], 1.0)
            g.memset(prefix[:, :], 1.0)
            g.memset(cmp_add[:, :], 0.0)
            link(g.memset(cmp_01[:, :], 1.0))
            select(ident[:, :], 1.0, 0, [[-1, P]], 1, ALU.not_equal)
            pool.sem_inc(s_const, 1)
            link(g.tensor_copy(identb[:, :], ident[:, :]))
            select(mask_causal[:, :], NEG, 0, [[-1, P]], 1)
            select(mask_window[:, :], NEG, -1, [[1, P]], -1)
            select(earlier[:, :], 0.0, -1, [[1, P]], -1)
            select(prefix[:, 0:NE], 0.0, -1, [[1, NE]], -1)
            select(prefix[:, NE:2 * NE], 0.0, 0, [[1, NE]], -1)
            c3 = [m[:, :].rearrange("p (b n) -> p b n", b=NB) for m in (cmp_add, cmp_01)]
            select(c3[0], NEG, -31, [[P, NB], [-16, 32]], 1)
            select(c3[1], 0.0, -31, [[P, NB], [-16, 32]], 1)
            io = dict(allow_small_or_imprecise_dtypes=True)
            link(g.iota(col128[:, :], [[1, P]], base=0, channel_multiplier=0, **io))
            link(g.iota(col32[:, :], [[1, 32]], base=0, channel_multiplier=0, **io))
            link(g.iota(tok_id[:, :], [[P, 2 * NB]], base=-int(EMPTY), channel_multiplier=1, **io))
            link(g.iota(slot0[:, :], [[TILE, NE]], base=0, channel_multiplier=0, **io))
            link(g.iota(over0[:, :], [[-TILE, NE]], base=NE * TILE - TILE, channel_multiplier=0, **io))
            link(g.iota(bounds[:, :], [[TILE, 8]], base=TILE, channel_multiplier=0, **io))
            pool.sem_inc(s_const, 1)

            pool.wait_ge(s_hm, 1)
            g.memset(cmp_in[0][:, :, 31:32], 0.0).then_inc(s_cz, 1)
            g.memset(cmp_in[1][:, :, 31:32], 0.0).then_inc(s_cz, 1)
            pool.wait_ge(s_small, SMALL)
            for b in range(NB):
                pool.wait_ge(s_vn, b + 1)
                g.tensor_tensor(v[:, b, :], v[:, b, :], v_gain, ALU.mult).then_inc(s_vg, 1)
            pool.wait_ge(s_cm, 1)
            link(g.memset(vbd, 0.0))
            pool.sem_inc(s_cz, 1)
            link(g.memset(qT[HD:P, 0], 0.0))
            link(g.memset(qT[0:HD, 1], 0.0))
            pool.sem_inc(s_cz, 2)
            pool.wait_ge(s_mtv, 3)
            g.affine_select(out=wsT, in_=wsT, compare_op=ALU.is_ge, fill=0.0, base=0,
                            pattern=[[0, 4], [1, P]], channel_multiplier=-1).then_inc(s_wsm, 1)

            def experts(l):
                pool.wait_ge(s_tab, l + 1)
                n_steps = pool.value_load(over_tab[0:1, MAX_OVER:MAX_OVER + 1], min_val=STEPS, max_val=MAX_STEPS)
                pool.wait_ge(s_st, 16 * NB * (l + 1))

                def gather(s, pair, at_least):
                    g.tensor_copy(gather_now[s][:, :], gather_at[:, bass.ds(pair, 1)]).then_inc(s_gn[l], 1)
                    pool.wait_ge(s_gn[l], at_least)
                    pool.sem_inc(s_pass, 1)
                    pool.indirect_dma_start(
                        out=xg[s], out_offset=None, in_=norm_dram,
                        in_offset=bass.IndirectOffsetOnAxis(ap=gather_now[s][:, 0:1], axis=0),
                        bounds_check=SEQ - 1, oob_is_err=False).then_inc(s_xg[l][s], 16)

                for s in range(2):
                    gather(s, s, s + 1)

                def scatter(j, s):
                    pool.sem_inc(s_yf[l], 1)
                    g.tensor_copy(scatter_now[s][:, :], scatter_at[:, bass.ds(2 * j + s, 1)]).then_inc(s_sn[l], 1)
                    pool.wait_ge(s_sn[l], 2 * j + s + 1)
                    pool.wait_ge(s_yr[l][s], 2 * (j + 1))
                    pool.sem_inc(s_pass, 1)
                    pool.indirect_dma_start(
                        out=out_dram,
                        out_offset=bass.IndirectOffsetOnAxis(ap=scatter_now[s][:, 0:1], axis=0),
                        in_=ys[s], in_offset=None,
                        bounds_check=2 * SEQ - 1, oob_is_err=False).then_inc(s_yo[l][s], 16)

                for s in range(2):
                    pool.wait_ge(s_xp[l], s + 1)
                    gather(s, 2 + s, s + 3)
                    scatter(0, s)
                with pool.Fori(1, MAX_STEPS) as j:
                    with pool.If(n_steps > j):
                        for s in range(2):
                            with pool.If(n_steps > j + 1):
                                pool.wait_ge(s_xp[l], 2 * j + s + 1)
                                gather(s, 2 * j + 2 + s, 2 * j + s + 3)
                            pool.wait_ge(s_yo[l][s], 16 * j)
                            scatter(j, s)
                for s in range(2):
                    pool.wait_ge(s_yo[l][s], 16 * n_steps)
                pool.sem_inc(s_all, 1)

            pool.wait_ge(s_x1, 2 * NB)
            for s in range(2):
                g.memset(xg[s], 0.0).then_inc(s_zero, 1)
            g.memset(band0[:, 3, 16:P], 1.0 / 16)
            for k in range(16):
                ins = g.memset(band0[:, 3, k:k + 1], 1.0 / (k + 1))
            link(ins)
            for i, w in enumerate((2, 4, 8, 16)):
                g.memset(band[:, i, :], 1.0 / w)
                g.memset(spill[:, i, :], 1.0 / w)
                if w < 16:
                    g.memset(band0[:, i, w:P], 1.0 / w)
                    g.tensor_copy(band0[:, i, 0:w], band0[:, 3, 0:w])
            link(g.memset(xg[0][:, 0:1], 0.0))
            for i, w in enumerate((2, 4, 8, 16)):
                for m in (band, band0):
                    select(m[:, i, :], 0.0, 0, [[1, P]], -1)
                    select(m[:, i, :], 0.0, w - 1, [[-1, P]], 1)
                    link(g.tensor_tensor(m[:, i, :], m[:, i, :], ident[:, :], ALU.subtract))
                select(spill[:, i, :], 0.0, w - 1 - P, [[-1, 16]], 1)
            pool.sem_inc(s_pool0, 1)
            pool.wait_ge(s_zero, 2)
            experts(0)

            pool.wait_ge(s_poolw, 48)
            scale = pool_sc.rearrange("p (g e) -> p g e", g=4)
            for i in range(2):
                wv = w_pool.rearrange("p (g i) e -> p g i e", g=4)[:, :, i, :]
                g.tensor_tensor(wv, wv, scale, ALU.mult).then_inc(s_ps, 1)
            link(g.tensor_tensor(pool_b, pool_b, pool_sc, ALU.mult))
            for b in range(NB):
                pool.wait_ge(s_xs[b], 3)
                g.tensor_tensor(x3[:, b, :], x3[:, b, :], pool_b, ALU.add).then_inc(s_pb, 1)
            experts(1)

        @block.scalar
        def _(act):
            a = nc.scalar
            count = [0]

            def link(ins):
                count[0] += 1
                ins.then_inc(s_av, 1)
                act.wait_ge(s_av, count[0])

            def norm(n):
                for b in range(NB):
                    act.wait_ge(*x_ready(n, b))
                    a.activation(xs[:, b, :], x3[:, b, :], ACT.Square,
                                 accum_out=ssq[:, n * NB + b:n * NB + b + 1]).then_inc(s_sq, 1)
                act.wait_ge(s_ms, n + 1)
                a.activation(std[:, n * NB:(n + 1) * NB], std[:, n * NB:(n + 1) * NB], ACT.Sqrt).then_inc(s_sd, 1)
                act.wait_ge(s_rs, n + 1)
                for b in (0, 2):
                    a.activation(xs[:, b, :], x3[:, b, :], ACT.Copy,
                                 scale=rstd[:, n * NB + b:n * NB + b + 1]).then_inc(s_xs[b], 1)

            def norm_evac(n):
                for b in range(NB):
                    act.wait_ge(s_tp, 2 * NB * TN[n] + 2 * b + 2)
                    for k in range(4):
                        ins = a.activation(xT[:, 4 + k, b * P:(b + 1) * P],
                                           bank(2 * (b % 2) + 1)[:, k * P:(k + 1) * P], ACT.Copy,
                                           scale=gain_v[:, n, 4 + k:5 + k])
                    ins.then_inc(s_ta, 1)


            norm(0)
            act.wait_ge(s_gain, 16)
            norm_evac(0)
            act.wait_ge(s_small, SMALL)
            link(a.activation(q_gain[:, :], q_gain[:, :], ACT.Copy, scale=HD ** -0.5))

            def proj_tile(ch, b):
                i = 4 * ch + b
                act.wait_ge(s_pj, i + 1)
                src = bank(4 + i % 4)
                if ch == 0:
                    a.activation(q[:, b, :].rearrange("p (i g d) -> p g i d", i=4, g=2),
                                 src.rearrange("p (g i d) -> p g i d", g=2, i=4), ACT.Copy).then_inc(s_pe_, 1)
                elif ch == 1:
                    a.activation(kv[:, b, 0:512], src, ACT.Copy).then_inc(s_pe_, 1)
                elif ch == 2:
                    a.activation(kv[:, b, 512:768], src[:, 0:256], ACT.Copy)
                    a.activation(gate[:, b * 24:(b + 1) * 24], src[:, 256:280], ACT.Exp, scale=-1.0).then_inc(s_pe_, 1)
                elif ch == 3:
                    a.activation(v[:, b, :], src, ACT.Gelu).then_inc(s_pe_, 1)
                else:
                    a.activation(u[:, b, :], src, ACT.Gelu).then_inc(s_pe_, 1)

            for ch in range(3):
                for b in range(NB):
                    proj_tile(ch, b)
            act.wait_ge(s_pe_, 12)
            a.activation(squares.rearrange("p (b c) -> p b c", b=NB), q, ACT.Square).then_inc(s_hs, 1)
            sq2 = squares2[:, 0:1024].rearrange("p (r b c) -> p r b c", r=2, b=NB)
            a.activation(sq2[:, 0], kv[:, :, 256:384], ACT.Square).then_inc(s_hs, 1)
            a.activation(sq2[:, 1], kv[:, :, 512:640], ACT.Square).then_inc(s_hs, 1)
            act.wait_ge(s_hm, 1)
            a.activation(hstd[:, :], hsq[:, :], ACT.Sqrt).then_inc(s_hd, 1)
            for b in range(NB):
                proj_tile(3, b)
            act.wait_ge(s_pe_, 16)
            a.activation(squares2.rearrange("p (b c) -> p b c", b=NB), v, ACT.Square).then_inc(s_vs, 1)
            act.wait_ge(s_vm, 1)
            a.activation(vstd[:, :], vsq[:, :], ACT.Sqrt).then_inc(s_vd, 1)

            def q_out(i):
                act.wait_ge(s_mt, 3 + i)
                for g in range(2):
                    r = slice(HD * g, HD * g + HD)
                    ins = a.activation(qT[r, g, i, :], bank(i % 2)[r, :], ACT.Copy, scale=q_gain[r, 0:1])
                ins.then_inc(s_mta, 1)

            proj_tile(4, 0)
            act.wait_ge(s_cm, 1)
            act.wait_ge(s_k2, 1)
            a.activation(csq[0:HD, 1:2], csq[0:HD, 0:1], ACT.Sqrt).then_inc(s_k3, 1)
            q_out(0)
            q_out(1)
            proj_tile(4, 1)
            q_out(2)
            q_out(3)
            proj_tile(4, 2)
            for r in range(2):
                act.wait_ge(s_mt, 8 + r)
                a.activation(kT[:, r, :], bank(2 + r), ACT.Copy, scale=k_gain[:, r:r + 1]).then_inc(s_mta, 1)
            act.wait_ge(s_c1, 1)
            a.activation(sc, sc, ACT.Exp).then_inc(s_c2, 1)
            proj_tile(4, 3)
            for j in range(2):
                act.wait_ge(s_c4, j + 1)
                if j == 1:
                    a.activation(pcT[:, 4:8, :], bank(3).rearrange("p (j t) -> p j t", j=4), ACT.Copy).then_inc(s_c5, 1)
            for b in range(NB):
                act.wait_ge(s_c6, b + 1)
                a.activation(yb[:, b, :], bank(b), ACT.Copy).then_inc(s_c7, 1)

            def exps(n):
                br, b, i = UNITS[n]
                width = P * key_blocks(UNITS[n])
                act.wait_ge(s_mx, n + 1)
                for h in range(2):
                    ins = a.activation(prob[:, n % 2, h, 0:width], bank(2 * (n % 2) + h)[:, 0:width], ACT.Exp,
                                       bias=nmax[:, 2 * n + h:2 * n + h + 1],
                                       accum_out=psum_row[:, 2 * n + h:2 * n + h + 1])
                ins.then_inc(s_ex, 1)

            banks_done = 0
            exps(0)
            exps(1)
            for n, un in enumerate(UNITS):
                nb = key_blocks(un)
                if nb > 2:
                    act.wait_ge(s_pt, banks_done + 2)
                    a.activation(pT[:, n % 2, 2:nb], bank(5)[:, 0:256 * (nb - 2)]
                                 .rearrange("p (a h t) -> p a h t", h=2, t=P), ACT.Copy).then_inc(s_pa, 1)
                banks_done += 1 + (nb > 2)
                if n + 2 < len(UNITS):
                    exps(n + 2)

            for k in range(1, KD, 2):
                act.wait_ge(s_yt, k + 1)
                a.activation(xT[:, k, :], bank(k), ACT.Copy).then_inc(s_yc, 1)

            def route(l):
                act.wait_ge(s_r1, l + 1)
                a.activation(rt["expo"], rt["exin"], ACT.Exp).then_inc(s_r2, 1)

            def experts(l):
                n = 1 + 2 * l
                act.wait_ge(s_tab, l + 1)
                n_steps = act.value_load(over_tab[0:1, MAX_OVER:MAX_OVER + 1], min_val=STEPS, max_val=MAX_STEPS)
                with act.Fori(0, MAX_STEPS) as j:
                    with act.If(n_steps > j):
                        for s in range(2):
                            act.wait_ge(s_xp[l], 2 * j + s + 1)
                            for k in range(4):
                                ins = a.activation(xgT[:, k, :], bank(0)[:, k * P:(k + 1) * P], ACT.Copy,
                                                   scale=gain_v[:, n, k:k + 1])
                            ins.then_inc(s_xe[l], 1)
                            act.wait_ge(s_gud[l][s], j + 1)
                            a.activation(sg, bank(2)[:, 0:FE], ACT.Silu).then_inc(s_sil[l], 1)
                            act.wait_ge(s_ht[l], 2 * j + s + 1)
                            a.activation(hidT, bank(3)[:, 0:2 * P].rearrange("p (j t) -> p j t", j=2), ACT.Copy)\
                             .then_inc(s_he[l], 1)
                            act.wait_ge(s_y[l][s], j + 1)
                            act.wait_ge(s_yf[l], 2 * j + s + 1)
                            a.activation(ys[s][:, 0:512], bank(4), ACT.Copy).then_inc(s_yr[l][s], 1)

            norm(1)
            norm_evac(1)
            route(0)
            experts(0)
            norm(2)
            for c in range(1, KD, 2):
                act.wait_ge(s_pt2, c + 1)
                a.activation(xT[:, c, :], bank(c), ACT.Copy, scale=gain_v[:, 2, c:c + 1]).then_inc(s_p2a, 1)
            norm(3)
            norm_evac(3)
            route(1)
            experts(1)

        @block.vector
        def _(dve):
            ve = nc.vector
            count = [0]

            def link(ins):
                count[0] += 1
                ins.then_inc(s_dv, 1)
                dve.wait_ge(s_dv, count[0])

            def tt(out, in0, in1, op):
                return ve.tensor_tensor(out, in0, in1, op)

            def bc(ap, axis, shape):
                return ap.unsqueeze(axis).to_broadcast(shape)

            def norm(n):
                dve.wait_ge(s_sq, NB * (n + 1))
                cols = slice(n * NB, (n + 1) * NB)
                ve.tensor_scalar(std[:, cols], ssq[:, cols], 1.0 / D, EPS, ALU.mult, ALU.add).then_inc(s_ms, 1)
                dve.wait_ge(s_sd, n + 1)
                ve.reciprocal(rstd[:, cols], std[:, cols]).then_inc(s_rs, 1)
                dve.wait_ge(s_rs, n + 1)
                for b in (1, 3):
                    ve.tensor_scalar(xs[:, b, :], x3[:, b, :], rstd[:, n * NB + b:n * NB + b + 1], None,
                                     ALU.mult).then_inc(s_xs[b], 1)

            def norm_evac(n):
                for b in range(NB):
                    dve.wait_ge(s_tp, 2 * NB * TN[n] + 2 * b + 1)
                    tt(xT[:, 0:4, b * P:(b + 1) * P], bank(2 * (b % 2)).rearrange("p (k t) -> p k t", k=4),
                       bc(gain_v[:, n, 0:4], 2, [P, 4, P]), ALU.mult).then_inc(s_tv, 1)

            norm(0)
            dve.wait_ge(s_gain, 16)
            norm_evac(0)
            dve.wait_ge(s_small, SMALL)

            dve.wait_ge(s_hs, 3)
            ve.tensor_reduce(hsq[:, 0:32], squares.rearrange("p (a d) -> p a d", d=HD), AX, ALU.add)
            link(ve.tensor_reduce(hsq[:, 32:48], squares2[:, 0:1024].rearrange("p (a d) -> p a d", d=HD), AX, ALU.add))
            ve.tensor_scalar(hsq[:, :], hsq[:, :], 1.0 / HD, EPS, ALU.mult, ALU.add).then_inc(s_hm, 1)
            link(ve.tensor_scalar(gate[:, :], gate[:, :], 1.0, None, ALU.add))
            ve.reciprocal(gate[:, :], gate[:, :])
            dve.wait_ge(s_hd, 1)
            link(ve.reciprocal(hrstd[:, :], hstd[:, :]))
            qv = q.rearrange("p b (h d) -> p b h d", d=HD)
            hv = hrstd[:, 0:32].rearrange("p (b h) -> p b h", b=NB)
            for b in range(NB):
                tt(qv[:, b], qv[:, b], bc(hv[:, b], 2, [P, NH, HD]), ALU.mult).then_inc(s_qk_n, 1)
            for r in range(2):
                c0 = 256 + 256 * r
                for b in range(NB):
                    kk = kv[:, b, c0:c0 + 128].rearrange("p (g d) -> p g d", g=2)
                    ks = hrstd[:, 32 + 8 * r + 2 * b:34 + 8 * r + 2 * b]
                    ins = tt(kk, kk, bc(ks, 2, [P, 2, HD]), ALU.mult)
                ins.then_inc(s_qk_n, 1)
            dve.wait_ge(s_cz, 2)
            for r in range(2):
                dve.wait_ge(s_mt, 1 + r)
                link(ve.tensor_copy(rawT[:, r, :], bank(r)))
                dve.sem_inc(s_mtv, 1)
                for half in range(2):
                    src = rawT[:, r, 16 * half:16 * half + 496].rearrange("p (n j) -> p j n", j=16)
                    ins = tt(cmp_in[r][:, 16 * half:16 * half + 16, 0:31], src,
                             bc(pe[:, 16 * half:16 * half + 16], 2, [P, 16, 31]), ALU.add)
                ins.then_inc(s_ci, 1)
            dve.wait_ge(s_vs, 1)
            link(ve.tensor_reduce(vsq[:, :], squares2.rearrange("p (a d) -> p a d", d=P), AX, ALU.add))
            ve.tensor_scalar(vsq[:, :], vsq[:, :], 1.0 / P, EPS, ALU.mult, ALU.add).then_inc(s_vm, 1)
            dve.wait_ge(s_vd, 1)
            link(ve.reciprocal(vrstd[:, :], vstd[:, :]))
            for b in range(NB):
                vv = v[:, b, :].rearrange("p (g d) -> p g d", g=4)
                tt(vv, vv, bc(vrstd[:, 4 * b:4 * b + 4], 2, [P, 4, P]), ALU.mult).then_inc(s_vn, 1)

            dve.wait_ge(s_cm, 1)
            ve.tensor_copy(kcn[0:32, 0:HD], bank(2)[0:32, 0:HD])
            link(ve.tensor_copy(kcn[32:64, 0:HD], bank(3)[32:64, 0:HD]))
            link(tt(kcsq[0:HD, :], kcn[0:HD, 0:HD], kcn[0:HD, 0:HD], ALU.mult))
            link(ve.tensor_reduce(csq[0:HD, 0:1], kcsq[0:HD, :], AX, ALU.add))
            ve.tensor_scalar(csq[0:HD, 0:1], csq[0:HD, 0:1], 1.0 / HD, EPS, ALU.mult, ALU.add).then_inc(s_k2, 1)
            dve.wait_ge(s_cz, 3)
            for gq in range(2):
                for h in range(4):
                    ins = ve.tensor_copy(vbd[32 * h:32 * h + 32, gq, HD * h:HD * h + HD],
                                         bank(2 + gq)[64 + 32 * gq:96 + 32 * gq, 0:HD])
            ins.then_inc(s_vb, 1)
            dve.wait_ge(s_k3, 1)
            link(ve.reciprocal(csq[0:HD, 2:3], csq[0:HD, 1:2]))
            link(ve.tensor_scalar(kcn[0:HD, 0:HD], kcn[0:HD, 0:HD], csq[0:HD, 2:3], None, ALU.mult))
            link(tt(kcn[0:HD, 0:HD], kcn[0:HD, 0:HD], kc_gain[0:HD, :], ALU.mult))
            ve.tensor_copy(kcn[0:HD, HD:2 * HD], kcn[0:HD, 0:HD]).then_inc(s_kn, 1)
            dve.wait_ge(s_kt, 1)
            ve.tensor_copy(kcT[0:64, :], bank(2)[0:64, 0:32])
            ve.tensor_copy(kcT[64:128, :], bank(2)[64:128, 32:64]).then_inc(s_kv, 1)
            dve.wait_ge(s_mt, 7)
            dve.wait_ge(s_vg, NB)
            ve.tensor_copy(wsT, bank(3).rearrange("p (g t) -> p g t", g=4)).then_inc(s_mtv, 1)
            c_add = cmp_add[:, :].rearrange("p (b n) -> p b n", b=NB)
            c_01 = cmp_01[:, :].rearrange("p (b n) -> p b n", b=NB)
            dve.wait_ge(s_cs, NB)
            for b in range(NB):
                ins = tt(sc[:, b].rearrange("p (g i) n -> p g i n", g=2),
                         ps[0][:, :, b * P:(b + 1) * P].rearrange("p g (i n) -> p g i n", i=4),
                         c_add[:, b].unsqueeze(1).unsqueeze(1).to_broadcast([P, 2, 4, 32]), ALU.add)
            link(ins)
            scf = sc.rearrange("p b h n -> p (b h) n")
            link(ve.tensor_reduce(cmax[:, :], scf, AX, ALU.max))
            tt(scf, scf, bc(cmax[:, :], 2, [P, NB * NH, 32]), ALU.subtract).then_inc(s_c1, 1)
            dve.wait_ge(s_c2, 1)
            link(ve.tensor_reduce(csum[:, :], scf[:, :, 0:31], AX, ALU.add))
            for b in range(NB):
                ins = tt(sc[:, b], sc[:, b], bc(c_01[:, b], 1, [P, NH, 32]), ALU.mult)
            link(ins)
            link(ve.reciprocal(csum[:, :], csum[:, :]))
            g4 = gate[:, :].rearrange("p (b h r) -> p b h r", b=NB, h=NH)
            link(tt(csum[:, :].rearrange("p (b h) -> p b h", b=NB), csum[:, :].rearrange("p (b h) -> p b h", b=NB),
                    g4[:, :, :, 0], ALU.mult))
            tt(scf, scf, bc(csum[:, :], 2, [P, NB * NH, 32]), ALU.mult).then_inc(s_c3, 1)
            dve.wait_ge(s_c4, 1)
            ve.tensor_copy(pcT[:, 0:4, :], bank(2).rearrange("p (j t) -> p j t", j=4)).then_inc(s_c5, 1)
            dve.wait_ge(s_pe_, 20)
            for gg in range(4):
                dve.wait_ge(s_zd, gg + 1)
                uu = u[:, :, gg * P:(gg + 1) * P]
                ve.scalar_tensor_tensor(uu, bank(4 + gg).rearrange("p (c d) -> p c d", c=NB), b_s[:, gg:gg + 1],
                                        uu, ALU.add, ALU.mult).then_inc(s_ya, 1)

            def maxes(n):
                width = P * key_blocks(UNITS[n])
                dve.wait_ge(s_qk, n + 1)
                ve.tensor_reduce(nmax[:, 2 * n:2 * n + 2], ps[n % 2][:, :, 0:width], AX, ALU.max, negate=True)\
                  .then_inc(s_mx, 1)

            banks_done = 0
            maxes(0)
            maxes(1)
            dve.wait_ge(s_c7, NB)
            for n, un in enumerate(UNITS):
                br, b, i = un
                nb = key_blocks(un)
                first = min(nb, 2)
                dve.wait_ge(s_pt, banks_done + 1)
                banks_done += 1 + (nb > 2)
                ve.tensor_copy(pT[:, n % 2, 0:first], bank(4)[:, 0:256 * first]
                               .rearrange("p (a h t) -> p a h t", h=2, t=P)).then_inc(s_pd, 1)
                if n + 2 < len(UNITS):
                    maxes(n + 2)
                cf = coef[:, 2 * n:2 * n + 2]
                link(ve.reciprocal(cf, psum_row[:, 2 * n:2 * n + 2]))
                link(tt(cf, cf, g4[:, b, :, 1 + br].rearrange("p (g i) -> p i g", g=2)[:, i, :], ALU.mult))
                dve.wait_ge(s_pv, n + 1)
                for h in range(2):
                    hh = 4 * h + i
                    dst = yb[:, b, hh * HD:(hh + 1) * HD]
                    ins = ve.scalar_tensor_tensor(dst, bank(6 + n % 2)[:, h * HD:(h + 1) * HD],
                                                  coef[:, 2 * n + h:2 * n + h + 1], dst, ALU.mult, ALU.add)
                ins.then_inc(s_o, 1)
                dve.wait_ge(s_o, n + 1)

            for k in range(0, KD, 2):
                dve.wait_ge(s_yt, k + 1)
                ve.tensor_copy(xT[:, k, :], bank(k)).then_inc(s_yv, 1)
            for i in range(2 * NB):
                dve.wait_ge(s_op, i + 1)
                dst = x3[:, i // 2, (i % 2) * 512:(i % 2) * 512 + 512]
                tt(dst, dst, bank(i), ALU.add).then_inc(s_x1, 1)

            def route(l):
                lgt = rt["lgt"].rearrange("p (b c) -> p b c", b=NB)
                dve.wait_ge(s_lg, l + 1)
                link(tt(lgt, bank(4)[:, 0:144].rearrange("p (b c) -> p b c", b=NB),
                        bc(r_bias[:, l * 36:(l + 1) * 36], 1, [P, NB, 36]), ALU.add))

                def first_max(src, n, mx, eq, tmp, mi, hot):
                    v3 = lambda ap: ap.rearrange("p (b n) -> p b n", b=NB)
                    link(ve.tensor_reduce(mx, src, AX, ALU.max))
                    link(tt(v3(eq), src, bc(mx, 2, [P, NB, n]), ALU.is_equal))
                    link(ve.scalar_tensor_tensor(v3(tmp), v3(eq), -64.0, bc(col32[:, 0:n], 1, [P, NB, n]),
                                                 ALU.mult, ALU.add))
                    link(ve.tensor_reduce(mi, v3(tmp), AX, ALU.min))
                    link(tt(v3(hot), v3(tmp), bc(mi, 2, [P, NB, n]), ALU.is_equal))

                first_max(lgt[:, :, 0:4], 4, rt["gmax"], rt["eq4"], rt["t4"], rt["gmin"], rt["ghot"])
                tt(rt["exin"][:, 0:16].rearrange("p (b n) -> p b n", b=NB), lgt[:, :, 0:4],
                   bc(rt["gmax"], 2, [P, NB, 4]), ALU.subtract)
                ghot = rt["ghot"].rearrange("p (b g) -> p b g", b=NB)
                le = lgt[:, :, 4:36].rearrange("p b (g e) -> p b g e", g=4)
                prod = rt["prod"].rearrange("p (b g e) -> p b g e", b=NB, g=4)
                link(tt(prod, le, bc(ghot, 3, [P, NB, 4, 8]), ALU.mult))
                les = rt["les"].rearrange("p (b e) -> p b e", b=NB)
                link(ve.tensor_reduce(les, prod.rearrange("p b g e -> p b e g"), AX, ALU.add))
                first_max(les, 8, rt["m1"], rt["eq8"], rt["t8"], rt["mi"], rt["h1"])
                link(ve.scalar_tensor_tensor(rt["les2"], rt["h1"], -3e38, rt["les"], ALU.mult, ALU.add))
                first_max(rt["les2"].rearrange("p (b e) -> p b e", b=NB), 8, rt["m2"], rt["eq8"], rt["t8"],
                          rt["mi"], rt["h2"])
                tt(rt["exin"][:, 16:20], rt["m2"], rt["m1"], ALU.subtract).then_inc(s_r1, 1)
                O = rt["O"].rearrange("p (c b g e) -> p c b g e", c=2, b=NB, g=4)
                for c, h in enumerate((rt["h1"], rt["h2"])):
                    ins = tt(O[:, c], bc(h.rearrange("p (b e) -> p b e", b=NB), 2, [P, NB, 4, 8]),
                             bc(ghot, 3, [P, NB, 4, 8]), ALU.mult)
                link(ins)
                tt(rt["Ob"], rt["O"][:, 0:128], rt["O"][:, 128:256], ALU.add).then_inc(s_r3, 1)
                dve.wait_ge(s_r2, l + 1)
                e2 = rt["expo"][:, 16:20]
                ve.tensor_reduce(rt["sE"], rt["expo"][:, 0:16].rearrange("p (b n) -> p b n", b=NB), AX, ALU.add)
                link(ve.tensor_scalar(rt["p1"], e2, 1.0, None, ALU.add))
                link(tt(rt["p1"], rt["p1"], rt["sE"], ALU.mult))
                link(ve.reciprocal(weight[:, 0:4], rt["p1"]))
                tt(weight[:, 4:8], weight[:, 0:4], e2, ALU.mult)
                dve.wait_ge(s_r4, l + 1)
                link(ve.tensor_copy(rt["cnt"][0:NE, :], bank(6)[0:NE, 0:1]))
                link(tt(rt["ovc"][0:NE, :], rt["cnt"][0:NE, :].to_broadcast([NE, 8]), bounds[0:NE, :], ALU.is_gt))
                link(ve.tensor_reduce(rt["ovs"][0:NE, :], rt["ovc"][0:NE, :], AX, ALU.add))
                ve.tensor_copy(rt["ovB"][0:NE, :], rt["ovs"][0:NE, :].to_broadcast([NE, P])).then_inc(s_r5, 1)
                dve.wait_ge(s_r6, l + 1)
                link(ve.scalar_tensor_tensor(rt["B"], bank(7)[:, 0:NE], float(TILE), over0[:, :], ALU.mult, ALU.add))
                rank = bank(5)[:, 0:128]
                v3 = lambda ap: ap.rearrange("p (b e) -> p b e", b=NB)
                ve.tensor_scalar(rt["ge"], rank, float(TILE), None, ALU.is_ge)
                link(tt(v3(rt["A"]), v3(rank), bc(slot0[:, :], 1, [P, NB, NE]), ALU.add))
                link(tt(v3(rt["ge"]), v3(rt["ge"]), bc(rt["B"], 1, [P, NB, NE]), ALU.mult))
                link(tt(rt["A"], rt["A"], rt["ge"], ALU.add))
                link(tt(rt["pS"].rearrange("p (c n) -> p c n", c=2), rt["O"].rearrange("p (c n) -> p c n", c=2),
                        bc(rt["A"], 1, [P, 2, 128]), ALU.mult))
                link(ve.tensor_reduce(rt["sl"], rt["pS"].rearrange("p (a e) -> p a e", e=NE), AX, ALU.add))
                link(ve.tensor_copy(rt["sli"], rt["sl"]))
                ve.tensor_single_scalar(rt["pmi"], rt["sli"], P - 1, ALU.bitwise_and)
                link(ve.tensor_single_scalar(rt["pci"], rt["sli"], 7, ALU.logical_shift_right))
                ve.tensor_copy(rt["pm"], rt["pmi"])
                link(ve.tensor_copy(rt["pc"], rt["pci"]))
                OA = rt["OA"].rearrange("p (a n) -> p a n", a=8)
                OC = rt["OC"].rearrange("p (a n) -> p a n", a=8)
                link(tt(OC, bc(col32[:, 0:PAIRS], 1, [P, 8, PAIRS]), bc(rt["pc"], 2, [P, 8, PAIRS]), ALU.is_equal))
                link(tt(OC, OC, bc(tok_id[:, :], 2, [P, 8, PAIRS]), ALU.mult))
                tt(OA, bc(col128[:, :], 1, [P, 8, P]), bc(rt["pm"], 2, [P, 8, P]), ALU.is_equal).then_inc(s_r7, 1)
                incl = rt["nst"]
                tb = rt["tabc"].rearrange("p (m e) -> p m e", m=MAX_OVER)
                link(ve.tensor_copy(rt["B"][0:1, :], bank(7)[0:1, NE:2 * NE]))
                tt(tb[0:1], bc(rt["B"][0:1, :], 1, [1, MAX_OVER, NE]), bc(col32[0:1, 0:MAX_OVER], 2, [1, MAX_OVER, NE]),
                   ALU.is_le)
                link(ve.tensor_scalar(incl[0:1, 0:4], bounds[0:1, 0:4], 1.0 / 16, -4.0, ALU.mult, ALU.add))
                link(tt(incl[0:1, 0:4], rt["B"][0:1, NE - 1:NE].to_broadcast([1, 4]), incl[0:1, 0:4], ALU.is_gt))
                ve.tensor_reduce(rt["tabr"][0:1, :], tb[0:1], AX, ALU.add)
                link(ve.tensor_reduce(rt["nsr"][0:1, :], incl[0:1, 0:4], AX, ALU.add))
                ve.tensor_scalar(over_tab[0:1, 0:MAX_OVER], rt["tabr"][0:1, :], float(NE - 1), None, ALU.min)
                ve.tensor_scalar(over_tab[0:1, MAX_OVER:MAX_OVER + 1], rt["nsr"][0:1, :], float(STEPS), None, ALU.add)
                dve.wait_ge(s_r8, l + 1)
                link(ve.tensor_scalar(rt["tabf"], bank(4)[:, 0:PAIRS], EMPTY, None, ALU.add))
                ve.tensor_copy(scatter_at[:, :], rt["tabf"])
                link(ve.tensor_scalar(rt["tge"], rt["tabf"], float(SEQ), None, ALU.is_ge))
                ve.memset(gather_at[:, PAIRS:PAIRS + 2], int(EMPTY))
                link(ve.scalar_tensor_tensor(gather_at[:, 0:PAIRS], rt["tge"], -float(SEQ), rt["tabf"],
                                             ALU.mult, ALU.add))
                dve.sem_inc(s_tab, 1)

            def experts(l):
                n = 1 + 2 * l
                n_steps = dve.value_load(over_tab[0:1, MAX_OVER:MAX_OVER + 1], min_val=STEPS, max_val=MAX_STEPS)
                with dve.Fori(0, MAX_STEPS) as j:
                    with dve.If(n_steps > j):
                        for s in range(2):
                            dve.wait_ge(s_xp[l], 2 * j + s + 1)
                            tt(xgT[:, 4:8, :], bank(1).rearrange("p (k t) -> p k t", k=4),
                               bc(gain_v[:, n, 4:8], 2, [P, 4, P]), ALU.mult).then_inc(s_xe[l], 1)
                            dve.wait_ge(s_sil[l], 2 * j + s + 1)
                            tt(hid, sg, bank(2)[:, FE:2 * FE], ALU.mult).then_inc(s_h[l], 1)
                            dve.wait_ge(s_y[l][s], j + 1)
                            dve.wait_ge(s_yf[l], 2 * j + s + 1)
                            ve.tensor_copy(ys[s][:, 512:1024], bank(5)).then_inc(s_yr[l][s], 1)
                for b in range(NB):
                    dve.wait_ge(s_yl[b], 32 * (l + 1))
                    link(ve.scalar_tensor_tensor(x3[:, b, :], YL[:, 0, b, :], weight[:, b:b + 1], x3[:, b, :],
                                                 ALU.mult, ALU.add))
                    ve.scalar_tensor_tensor(x3[:, b, :], YL[:, 1, b, :], weight[:, 4 + b:5 + b], x3[:, b, :],
                                            ALU.mult, ALU.add).then_inc(s_cb, 1)

            norm(1)
            norm_evac(1)
            route(0)
            experts(0)
            norm(2)
            for c in range(0, KD, 2):
                dve.wait_ge(s_pt2, c + 1)
                ve.tensor_scalar(xT[:, c, :], bank(c), gain_v[:, 2, c:c + 1], None, ALU.mult).then_inc(s_p2v, 1)
            for b in range(NB):
                dve.wait_ge(s_po, b + 1)
                dve.wait_ge(s_pb, b + 1)
                xb = X[:, b * D:(b + 1) * D].rearrange("p (a n) -> p a n", a=2)
                tt(xb, xb, ps[b][:, :, :], ALU.add).then_inc(s_x3, 1)
            norm(3)
            norm_evac(3)
            route(1)
            experts(1)

        @block.tensor
        def _(pe_):
            te = nc.tensor
            mm = te.matmul

            def norm_transpose(n):
                for b in range(NB):
                    pe_.wait_ge(s_xs[b], n + 1)
                    if b >= 2:
                        pe_.wait_ge(s_tv, NB * TN[n] + b - 1)
                        pe_.wait_ge(s_ta, NB * TN[n] + b - 1)
                    xv = xs[:, b, :].rearrange("p (c k) -> p k c", k=KD)
                    for k in range(KD):
                        ins = te.transpose(bank(2 * (b % 2) + k // 4)[:, (k % 4) * P:(k % 4 + 1) * P],
                                           xv[:, k, :], ident[:, :])
                        if k % 4 == 3:
                            ins.then_inc(s_tp, 1)

            pe_.wait_ge(s_const, 1)
            norm_transpose(0)
            pe_.wait_ge(s_tv, NB)
            pe_.wait_ge(s_ta, NB)

            def project(ch, b):
                n = CH[ch][2]
                w = win[ch % 2][:, 0:KD * n].rearrange("p (k n) -> p k n", k=KD)
                i = 4 * ch + b
                if b == 0:
                    pe_.wait_ge(s_w[ch], 16)
                if i >= 4:
                    pe_.wait_ge(s_pe_, i - 3)
                for k in range(KD):
                    ins = mm(bank(4 + i % 4)[:, 0:n], xT[:, k, b * P:(b + 1) * P], w[:, k, :],
                             start=(k == 0), stop=(k == KD - 1))
                ins.then_inc(s_pj, 1)

            def transpose_blocks(o, src, c0):
                for b in range(NB):
                    ins = te.transpose(o[:, b * P:(b + 1) * P], src[:, b, c0:c0 + P], ident[:, :])
                ins.then_inc(s_mt, 1)

            for ch in range(3):
                for b in range(NB):
                    project(ch, b)
            pe_.wait_ge(s_pe_, 8)
            transpose_blocks(bank(0), kv, 0)
            transpose_blocks(bank(1), kv, P)
            for b in range(NB):
                project(3, b)
            pe_.wait_ge(s_wcmp, 64)
            pe_.wait_ge(s_ci, 2)
            for l in range(32):
                for w in range(2):
                    for g in range(2):
                        r = slice(64 * g, 64 * g + 64)
                        o = 64 * w + 32 * g
                        ins = mm(bank(2 + g)[o:o + 32, 0:HD], cmp_in[w][r, l, :], wcmp[r, w, l, :],
                                 start=(l == 0), stop=(l == 31), tile_position=(64 * g, o))
            ins.then_inc(s_cm, 1)
            project(4, 0)
            pe_.wait_ge(s_qk_n, 6)
            pe_.wait_ge(s_mtv, 2)
            transpose_blocks(bank(0), q, 0)
            transpose_blocks(bank(1), q, P)
            project(4, 1)
            pe_.wait_ge(s_kn, 1)
            pe_.wait_ge(s_vb, 1)
            te.transpose(bank(2)[:, 0:64], kcn[0:64, :], ident[0:64, 0:64]).then_inc(s_kt, 1)
            pe_.wait_ge(s_mta, 1)
            transpose_blocks(bank(0), q, 2 * P)
            pe_.wait_ge(s_mta, 2)
            transpose_blocks(bank(1), q, 3 * P)
            pe_.wait_ge(s_ws, 16)
            for gg in range(4):
                ins = te.transpose(bank(3)[:, gg * P:(gg + 1) * P], ws_raw[:, gg, :], ident[:, :])
            ins.then_inc(s_mt, 1)
            project(4, 2)
            pe_.wait_ge(s_kv, 1)
            transpose_blocks(bank(2), kv, 256)
            pe_.wait_ge(s_mtv, 3)
            transpose_blocks(bank(3), kv, 512)
            pe_.wait_ge(s_mta, 4)
            pe_.wait_ge(s_cz, 5)
            for b in range(NB):
                for i in range(4):
                    for g in range(2):
                        c0 = b * P + i * 32
                        ins = mm(bank(g)[:, c0:c0 + 32], qT[:, g, i, b * P:(b + 1) * P], kcT[:, :],
                                 start=True, stop=True)
                ins.then_inc(s_cs, 1)
            project(4, 3)
            pe_.wait_ge(s_wsm, 1)
            pe_.wait_ge(s_vg, NB)
            for gg in range(4):
                pe_.wait_ge(s_pe_, 17 + gg)
                mm(bank(4 + gg), wsT[:, gg, :], v[:, :, gg * P:(gg + 1) * P], start=True, stop=True).then_inc(s_zd, 1)
            pe_.wait_ge(s_c3, 1)
            pe_.wait_ge(s_mta, 6)
            for j in range(8):
                b, g = j // 2, j % 2
                ins = te.transpose(bank(2 + j // 4)[:, (j % 4) * P:(j % 4 + 1) * P],
                                   sc[:, b, 4 * g:4 * g + 4, :].rearrange("p h n -> p (h n)"), ident[:, :])
                if j % 4 == 3:
                    ins.then_inc(s_c4, 1)
            pe_.wait_ge(s_c5, 2)
            for b in range(NB):
                for g in range(2):
                    ins = mm(bank(b)[:, g * 256:(g + 1) * 256], pcT[:, 2 * b + g, :], vbd[:, g, :],
                             start=True, stop=True)
                ins.then_inc(s_c6, 1)

            def scores(n):
                br, b, i = UNITS[n]
                f = first_key(br, b)
                nb = key_blocks(UNITS[n])
                if n >= 2:
                    pe_.wait_ge(s_ex, n - 1)
                else:
                    pe_.wait_ge(s_c7, 2 * n + 2)
                for h in range(2):
                    mm(bank(2 * (n % 2) + h)[:, 0:P * nb], qT[:, h, i, b * P:(b + 1) * P],
                       kT[:, br, f * P:(b + 1) * P], start=True, stop=False)
                for h in range(2):
                    o = bank(2 * (n % 2) + h)
                    edge = br == 1 and b >= 2
                    ins = mm(o[:, P * (nb - 1):P * nb], identb[:, :], mask_causal[:, :], start=False, stop=not edge)
                    if edge:
                        ins = mm(o[:, 0:P], identb[:, :], mask_window[:, :], start=False, stop=True)
                ins.then_inc(s_qk, 1)

            pe_.wait_ge(s_const, 2)
            pe_.wait_ge(s_ya, 4)
            scores(0)
            scores(1)
            n_act = 0
            for n, un in enumerate(UNITS):
                br, b, i = un
                f, nb = first_key(br, b), key_blocks(un)
                pe_.wait_ge(s_ex, n + 1)
                for a in range(nb):
                    for h in range(2):
                        ins = te.transpose(bank(4 + a // 2)[:, (a % 2) * 256 + h * P:(a % 2) * 256 + (h + 1) * P],
                                           prob[:, n % 2, h, a * P:(a + 1) * P], ident[:, :])
                    if a == min(nb, 2) - 1 or (a == nb - 1):
                        ins.then_inc(s_pt, 1)
                if n + 2 < len(UNITS):
                    scores(n + 2)
                n_act += nb > 2
                pe_.wait_ge(s_pd, n + 1)
                if nb > 2:
                    pe_.wait_ge(s_pa, n_act)
                if n >= 2:
                    pe_.wait_ge(s_o, n - 1)
                for h in range(2):
                    for a in range(nb):
                        vc = 384 + 256 * br + h * HD
                        ins = mm(bank(6 + n % 2)[:, h * HD:(h + 1) * HD], pT[:, n % 2, a, h, :],
                                 kv[:, f + a, vc:vc + HD], start=(a == 0), stop=(a == nb - 1))
                ins.then_inc(s_pv, 1)

            pe_.wait_ge(s_o, len(UNITS))
            for k in range(KD):
                for b in range(NB):
                    src = (u if k < 4 else yb)[:, b, (k % 4) * P:(k % 4 + 1) * P]
                    ins = te.transpose(bank(k)[:, b * P:(b + 1) * P], src, ident[:, :])
                ins.then_inc(s_yt, 1)
            pe_.wait_ge(s_wout, 16)
            pe_.wait_ge(s_yv, 4)
            pe_.wait_ge(s_yc, 4)
            for i in range(2 * NB):
                b, half = i // 2, i % 2
                for k in range(KD):
                    ins = mm(bank(i), xT[:, k, b * P:(b + 1) * P], wout[:, k, half * 512:(half + 1) * 512],
                             start=(k == 0), stop=(k == KD - 1))
                ins.then_inc(s_op, 1)

            def route(l):
                wr = w_r[:, :].rearrange("p (k c) -> p k c", k=KD)
                pe_.wait_ge(s_wr, 32 * (l + 1))
                n = 1 + 2 * l
                pe_.wait_ge(s_tv, NB * (TN[n] + 1))
                pe_.wait_ge(s_ta, NB * (TN[n] + 1))
                for b in range(NB):
                    for k in range(KD):
                        ins = mm(bank(4)[:, b * 36:(b + 1) * 36], xT[:, k, b * P:(b + 1) * P], wr[:, k, :],
                                 start=(k == 0), stop=(k == KD - 1))
                ins.then_inc(s_lg, 1)
                pe_.wait_ge(s_r3, l + 1)
                Ob = rt["Ob"].rearrange("p (b e) -> p b e", b=NB)
                for b in range(NB):
                    mm(bank(6)[0:NE, 0:1], Ob[:, b, :], ones[:, 0:1], start=(b == 0), stop=(b == NB - 1))
                for b in range(NB):
                    for b2 in range(b + 1):
                        ins = mm(bank(5)[:, b * NE:(b + 1) * NE], (earlier if b2 == b else ones)[:, :],
                                 Ob[:, b2, :], start=(b2 == 0), stop=(b2 == b))
                ins.then_inc(s_r4, 1)
                pe_.wait_ge(s_r5, l + 1)
                mm(bank(7)[:, 0:2 * NE], rt["ovB"][0:NE, :], prefix[:, :], start=True, stop=True).then_inc(s_r6, 1)
                pe_.wait_ge(s_r7, l + 1)
                OA = rt["OA"].rearrange("p (a n) -> p a n", a=8)
                OC = rt["OC"].rearrange("p (a n) -> p a n", a=8)
                for a in range(8):
                    ins = mm(bank(4)[:, 0:PAIRS], OA[:, a, :], OC[:, a, :], start=(a == 0), stop=(a == 7))
                ins.then_inc(s_r8, 1)

            def experts(l):
                pe_.wait_ge(s_tab, l + 1)
                n_steps = pe_.value_load(over_tab[0:1, MAX_OVER:MAX_OVER + 1], min_val=STEPS, max_val=MAX_STEPS)
                with pe_.Fori(0, MAX_STEPS) as j:
                    with pe_.If(n_steps > j):
                        for s in range(2):
                            pe_.wait_ge(s_xg[l][s], 16 * (j + 1))
                            xv = xg[s].rearrange("p (c k) -> p k c", k=KD)
                            for k in range(KD):
                                ins = te.transpose(bank(k // 4)[:, (k % 4) * P:(k % 4 + 1) * P], xv[:, k, :],
                                                   ident[:, :])
                            ins.then_inc(s_xp[l], 1)
                            pe_.wait_ge(s_xe[l], 4 * j + 2 * s + 2)
                            pe_.wait_ge(s_gul[l][s], 64 * (j + 1))
                            for k in range(KD):
                                for a in range(2):
                                    ins = mm(bank(2)[64 * a:64 * a + 64, :], xgT[:, k, 64 * a:64 * a + 64],
                                             gu[s][:, a, :, k * FE:(k + 1) * FE],
                                             start=(k == 0), stop=(k == KD - 1))
                            ins.then_inc(s_gud[l][s], 1)
                            pe_.wait_ge(s_h[l], 2 * j + s + 1)
                            hv = hid.rearrange("p (c j) -> p j c", j=2)
                            for jj in range(2):
                                ins = te.transpose(bank(3)[:, jj * P:(jj + 1) * P], hv[:, jj, :], ident[:, :])
                            ins.then_inc(s_ht[l], 1)
                            pe_.wait_ge(s_he[l], 2 * j + s + 1)
                            pe_.wait_ge(s_dnl[l][s], 32 * (j + 1))
                            for half in range(2):
                                for jj in range(2):
                                    for a in range(2):
                                        c0 = jj * D + half * 512
                                        ins = mm(bank(4 + half)[64 * a:64 * a + 64, :], hidT[:, jj, 64 * a:64 * a + 64],
                                                 dn[s][:, a, c0:c0 + 512], start=(jj == 0), stop=(jj == 1))
                            ins.then_inc(s_y[l][s], 1)

            norm_transpose(1)
            route(0)
            experts(0)
            pe_.wait_ge(s_pool0, 1)
            for b in range(NB):
                pe_.wait_ge(s_xs[b], 3)
            for c in range(KD):
                g, i = c // 2, c % 2
                xv = xs[:, :, g * 256:(g + 1) * 256].rearrange("p b (c i) -> p b i c", i=2)[:, :, i, :]
                for b in range(NB):
                    ins = mm(bank(c)[:, b * P:(b + 1) * P], xv[:, b, :], (band0 if b == 0 else band)[:, g, :],
                             start=True, stop=(b == 0))
                    if b:
                        ins = mm(bank(c)[:, b * P:b * P + 16], xv[:, b - 1, :], spill[:, g, :], start=False, stop=True)
                ins.then_inc(s_pt2, 1)
            pe_.wait_ge(s_p2v, 4)
            pe_.wait_ge(s_p2a, 4)
            pe_.wait_ge(s_ps, 2)
            for b in range(NB):
                for g in range(4):
                    for i in range(2):
                        ins = mm(ps[b][:, g // 2, (g % 2) * 256:(g % 2) * 256 + 256], xT[:, 2 * g + i, b * P:(b + 1) * P],
                                 w_pool[:, 2 * g + i, :], start=(i == 0), stop=(i == 1))
                ins.then_inc(s_po, 1)
            norm_transpose(3)
            route(1)
            experts(1)


_INS = ['x', 'mix_norm_even', 'w_in', 'a_v_gain', 'a_w_s', 'a_b_s', 'q_gain', 'k_gain', 'cmp_pe', 'w_cmp_k',
        'w_cmp_v', 'w_out', 'mix_norm_odd', 'w_pool', 'b_pool', 'pool_scale', 'ffn_norm', 'w_router_group',
        'b_router_group', 'w_router_expert', 'b_router_expert', 'w_exp_gate', 'w_exp_up', 'w_exp_down']


def kernel(**inputs):
    import numpy as _np
    import concourse.bacc as _bacc
    from concourse import mybir as _mybir
    from concourse.bass_utils import run_bass_kernel_spmd as _run

    nc = _bacc.Bacc("TRN2", target_bir_lowering=False, num_devices=1)
    arrays, tensors = {}, {}
    for name in _INS:
        a = _np.ascontiguousarray(inputs[name])
        arrays[f"in_{name}_dram"] = a
        tensors[name] = nc.dram_tensor(f"in_{name}_dram", a.shape, _mybir.dt.from_np(a.dtype),
                                       kind="ExternalInput").ap()
    tensors["out"] = nc.dram_tensor("out_0_dram", (1, SEQ, D), _mybir.dt.float32, kind="ExternalOutput").ap()
    build(nc, tensors)
    r = _run(nc, [arrays], core_ids=[0])
    return r.results[0]["out_0_dram"]
```
